# Optimizing a Trainium2 kernel written in Bass

```python
import jax, jax.numpy as jnp
from jax import lax
import numpy as np

D_MODEL = 2048
BATCH = 1
SEQ = 256
DEPTH = 1

D_CONV = D_MODEL // 2
CONV_GROUPS = 16
CONV_WIDTH = 3
D_ATTN = D_MODEL - D_CONV
N_HEADS = 8
HEAD_DIM = D_ATTN // N_HEADS
D_MIX = D_CONV + D_ATTN
D_IN = 4 * D_CONV + 4 * D_ATTN
MOBA_BLOCK = 256
MOBA_TOPK = 3
Q_CHUNK = 64
EPS = 1e-6


def rms_norm(x, gain):
    xf = x.astype(jnp.float32)
    y = xf * lax.rsqrt(jnp.mean(xf * xf, axis=-1, keepdims=True) + EPS)
    return (y * gain.astype(jnp.float32)).astype(x.dtype)

def short_gated_conv(h, b_gate, c_gate, conv_w):
    seq = h.shape[1]
    u = c_gate * h
    u_pad = jnp.pad(u, ((0, 0), (CONV_WIDTH - 1, 0), (0, 0)))
    conv = u_pad[:, 0:seq] * conv_w[0]
    for tap in range(1, CONV_WIDTH):
        conv = conv + u_pad[:, tap:tap + seq] * conv_w[tap]
    return b_gate * conv

def moba_attention(q, k, v):
    bsz, n_heads, seq, hd = q.shape
    n_blocks = -(-seq // MOBA_BLOCK)
    pad = n_blocks * MOBA_BLOCK - seq
    k_pad = jnp.pad(k, ((0, 0), (0, 0), (0, pad), (0, 0)))
    v_pad = jnp.pad(v, ((0, 0), (0, 0), (0, pad), (0, 0)))
    k_blocks = k_pad.reshape(bsz, n_heads, n_blocks, MOBA_BLOCK, hd)
    v_blocks = v_pad.reshape(bsz, n_heads, n_blocks, MOBA_BLOCK, hd)
    k_mean = jnp.mean(k_blocks.astype(jnp.float32), axis=3)
    k_sel = min(MOBA_TOPK, n_blocks)
    scale = hd ** -0.5
    n_chunks = seq // Q_CHUNK
    q_chunks = q.reshape(bsz, n_heads, n_chunks, Q_CHUNK, hd).transpose(2, 0, 1, 3, 4)
    b_idx = jnp.arange(bsz)[:, None, None]
    h_idx = jnp.arange(n_heads)[None, :, None]
    block_ids = jnp.arange(n_blocks)
    slot_ids = jnp.arange(k_sel)
    key_offsets = jnp.arange(MOBA_BLOCK)

    def chunk_fn(args):
        ci, q_blk = args
        start = ci * Q_CHUNK
        own = start // MOBA_BLOCK
        q_pos = start + jnp.arange(Q_CHUNK)
        gate = jnp.einsum('bhqd,bhnd->bhqn', q_blk.astype(jnp.float32), k_mean)
        gate = jnp.where(block_ids < own, gate, -jnp.inf)
        _, sel = lax.top_k(gate, k_sel)
        sel_valid = slot_ids < own
        k_own = lax.dynamic_index_in_dim(k_blocks, own, axis=2, keepdims=False)
        v_own = lax.dynamic_index_in_dim(v_blocks, own, axis=2, keepdims=False)
        s_own = jnp.einsum('bhqd,bhkd->bhqk', q_blk, k_own).astype(jnp.float32) * scale
        k_pos = own * MOBA_BLOCK + key_offsets
        s_own = jnp.where(k_pos[None, :] <= q_pos[:, None], s_own, -jnp.inf)
        scores = []
        for slot in range(k_sel):
            k_g = k_blocks[b_idx, h_idx, sel[..., slot]]
            s = jnp.einsum('bhqd,bhqkd->bhqk', q_blk, k_g).astype(jnp.float32) * scale
            scores.append(jnp.where(sel_valid[slot], s, -jnp.inf))
        scores.append(s_own)
        probs = jax.nn.softmax(jnp.concatenate(scores, axis=-1), axis=-1).astype(v.dtype)
        out = jnp.einsum('bhqk,bhkd->bhqd', probs[..., k_sel * MOBA_BLOCK:], v_own)
        for slot in range(k_sel):
            v_g = v_blocks[b_idx, h_idx, sel[..., slot]]
            p_slot = probs[..., slot * MOBA_BLOCK:(slot + 1) * MOBA_BLOCK]
            out = out + jnp.einsum('bhqk,bhqkd->bhqd', p_slot, v_g)
        return out.astype(q.dtype)

    outs = lax.map(chunk_fn, (jnp.arange(n_chunks), q_chunks))
    return outs.transpose(1, 2, 0, 3, 4).reshape(bsz, n_heads, seq, hd)

def first_inputs(seed: int = 0) -> dict:
    key = jax.random.key(seed)
    ks = jax.random.split(key, 9)
    x = jax.random.normal(ks[0], (BATCH, SEQ, D_MODEL), jnp.float32)
    norm_gain = 1.0 + 0.1 * jax.random.normal(ks[1], (DEPTH, D_MODEL), jnp.float32)
    w_in = jax.random.normal(ks[2], (DEPTH, D_MODEL, D_IN), jnp.float32) * D_MODEL ** -0.5
    conv_w = jax.random.normal(ks[3], (DEPTH, CONV_WIDTH, D_CONV), jnp.float32) * CONV_WIDTH ** -0.5
    q_norm_gain = 1.0 + 0.1 * jax.random.normal(ks[4], (DEPTH, HEAD_DIM), jnp.float32)
    k_norm_gain = 1.0 + 0.1 * jax.random.normal(ks[5], (DEPTH, HEAD_DIM), jnp.float32)
    conv_out_gain = 1.0 + 0.1 * jax.random.normal(ks[6], (DEPTH, D_CONV), jnp.float32)
    attn_out_gain = 1.0 + 0.1 * jax.random.normal(ks[7], (DEPTH, D_ATTN), jnp.float32)
    w_out = jax.random.normal(ks[8], (DEPTH, D_MIX, D_MODEL), jnp.float32) * D_MIX ** -0.5
    return {"x": x, "norm_gain": norm_gain, "w_in": w_in, "conv_w": conv_w,
            "q_norm_gain": q_norm_gain, "k_norm_gain": k_norm_gain,
            "conv_out_gain": conv_out_gain, "attn_out_gain": attn_out_gain, "w_out": w_out}

def first_block(x, norm_gain, w_in, conv_w, q_norm_gain, k_norm_gain, conv_out_gain, attn_out_gain, w_out):
    bsz, seq, _ = x.shape
    split_points = [D_CONV, 2 * D_CONV, 3 * D_CONV, 4 * D_CONV,
                    4 * D_CONV + D_ATTN, 4 * D_CONV + 2 * D_ATTN, 4 * D_CONV + 3 * D_ATTN]
    for layer in range(DEPTH):
        h = rms_norm(x, norm_gain[layer])
        proj = jnp.einsum('bsd,de->bse', h, w_in[layer])
        h_conv, b_gate, c_gate, z_conv, q, k, v, z_attn = jnp.split(proj, split_points, axis=-1)
        y_conv = short_gated_conv(h_conv, b_gate, c_gate, conv_w[layer])
        y_conv = rms_norm(y_conv, conv_out_gain[layer]) * jax.nn.silu(z_conv)
        q = rms_norm(q.reshape(bsz, seq, N_HEADS, HEAD_DIM), q_norm_gain[layer]).transpose(0, 2, 1, 3)
        k = rms_norm(k.reshape(bsz, seq, N_HEADS, HEAD_DIM), k_norm_gain[layer]).transpose(0, 2, 1, 3)
        v = v.reshape(bsz, seq, N_HEADS, HEAD_DIM).transpose(0, 2, 1, 3)
        y_attn = moba_attention(q, k, v).transpose(0, 2, 1, 3).reshape(bsz, seq, D_ATTN)
        y_attn = rms_norm(y_attn, attn_out_gain[layer]) * jax.nn.silu(z_attn)
        y = jnp.concatenate([y_conv, y_attn], axis=-1)
        x = x + jnp.einsum('bse,ed->bsd', y, w_out[layer])
    return x


CTX_LEN = 256
GRID_W = 64
HEAD_DIM_2 = 64
N_Q_HEADS = D_MODEL // (2 * HEAD_DIM_2)
N_KV_HEADS = N_Q_HEADS // 4
ATTN_WIDTH = N_Q_HEADS * HEAD_DIM_2
KV_WIDTH = N_KV_HEADS * HEAD_DIM_2
POOL_WINDOWS = (2, 4, 8, 16)
POOL_GROUPS = len(POOL_WINDOWS)
POOL_WIDTH = D_MODEL - ATTN_WIDTH
POOL_GROUP_DIM = POOL_WIDTH // POOL_GROUPS
MIX_WIDTH = ATTN_WIDTH + POOL_WIDTH
IN_WIDTH = ATTN_WIDTH + 2 * KV_WIDTH + POOL_WIDTH
D_FF = 4 * D_MODEL
WINDOW = 128
BLOCK = 128
ROPE_BASE = 10000.0
N_MOD = 6
NEG_INF = -1e30


def rms_norm_2(x, w):
    xf = x.astype(jnp.float32)
    y = xf * lax.rsqrt(jnp.mean(xf * xf, axis=-1, keepdims=True) + EPS)
    return (y * w.astype(jnp.float32)).astype(x.dtype)

def ada_modulation(cond, w, b):
    m = jax.nn.silu(cond) @ w + b
    return jnp.split(m[..., None, :], N_MOD, axis=-1)

def modulate(h, shift, scale):
    return h * (1.0 + scale) + shift

def split_projection(p):
    B, L, _ = p.shape
    q, k, v, u = jnp.split(p, [ATTN_WIDTH, ATTN_WIDTH + KV_WIDTH, ATTN_WIDTH + 2 * KV_WIDTH], axis=-1)
    return (q.reshape(B, L, N_Q_HEADS, HEAD_DIM_2), k.reshape(B, L, N_KV_HEADS, HEAD_DIM_2),
            v.reshape(B, L, N_KV_HEADS, HEAD_DIM_2), u)

def axial_positions(seq_len):
    rows = seq_len // GRID_W
    row = jnp.broadcast_to(jnp.arange(rows)[:, None], (rows, GRID_W)).reshape(-1)
    col = jnp.broadcast_to(jnp.arange(GRID_W)[None, :], (rows, GRID_W)).reshape(-1)
    return row, col

def rope_2d(x, row, col):
    half = HEAD_DIM_2 // 2
    inv_freq = ROPE_BASE ** (-jnp.arange(0, half, 2, dtype=jnp.float32) / half)

    def rot(xa, pos):
        ang = pos.astype(jnp.float32)[:, None] * inv_freq[None, :]
        cos = jnp.cos(ang)[None, :, None, :]
        sin = jnp.sin(ang)[None, :, None, :]
        x1, x2 = jnp.split(xa, 2, axis=-1)
        return jnp.concatenate([x1 * cos - x2 * sin, x1 * sin + x2 * cos], axis=-1)

    xf = x.astype(jnp.float32)
    out = jnp.concatenate([rot(xf[..., :half], row), rot(xf[..., half:], col)], axis=-1)
    return out.astype(x.dtype)

def latent_window_attention(q, k, v, k_ctx, v_ctx, sink):
    B, L, H, D = q.shape
    G = H // N_KV_HEADS
    nb = L // BLOCK
    scale = HEAD_DIM_2 ** -0.5
    qb = q.reshape(B, nb, BLOCK, N_KV_HEADS, G, D)
    pad = ((0, 0), (BLOCK, BLOCK), (0, 0), (0, 0))
    kp = jnp.pad(k, pad).reshape(B, nb + 2, BLOCK, N_KV_HEADS, D)
    vp = jnp.pad(v, pad).reshape(B, nb + 2, BLOCK, N_KV_HEADS, D)
    kb = jnp.concatenate([kp[:, :-2], kp[:, 1:-1], kp[:, 2:]], axis=2)
    vb = jnp.concatenate([vp[:, :-2], vp[:, 1:-1], vp[:, 2:]], axis=2)
    s_win = jnp.einsum('bnqhgd,bnkhd->bhgnqk', qb, kb).astype(jnp.float32) * scale
    blk = jnp.arange(nb)[:, None, None] * BLOCK
    qpos = blk + jnp.arange(BLOCK)[None, :, None]
    kpos = blk - BLOCK + jnp.arange(3 * BLOCK)[None, None, :]
    valid = (jnp.abs(qpos - kpos) <= WINDOW) & (kpos >= 0) & (kpos < L)
    s_win = jnp.where(valid, s_win, NEG_INF)
    s_ctx = jnp.einsum('bnqhgd,bchd->bhgnqc', qb, k_ctx).astype(jnp.float32) * scale
    s_sink = jnp.broadcast_to(sink.astype(jnp.float32).reshape(N_KV_HEADS, G)[None, :, :, None, None, None],
                              s_win.shape[:-1] + (1,))
    p = jax.nn.softmax(jnp.concatenate([s_win, s_ctx, s_sink], axis=-1), axis=-1)
    n_win = 3 * BLOCK
    n_ctx = k_ctx.shape[1]
    p_win = p[..., :n_win].astype(v.dtype)
    p_ctx = p[..., n_win:n_win + n_ctx].astype(v.dtype)
    out = (jnp.einsum('bhgnqk,bnkhd->bnqhgd', p_win, vb)
           + jnp.einsum('bhgnqc,bchd->bnqhgd', p_ctx, v_ctx))
    return out.reshape(B, L, H * D)

def context_attention(q, k, v, sink):
    B, C, H, D = q.shape
    G = H // N_KV_HEADS
    qg = q.reshape(B, C, N_KV_HEADS, G, D)
    s = jnp.einsum('bqhgd,bkhd->bhgqk', qg, k).astype(jnp.float32) * (HEAD_DIM_2 ** -0.5)
    s_sink = jnp.broadcast_to(sink.astype(jnp.float32).reshape(N_KV_HEADS, G)[None, :, :, None, None],
                              s.shape[:-1] + (1,))
    p = jax.nn.softmax(jnp.concatenate([s, s_sink], axis=-1), axis=-1)[..., :C].astype(v.dtype)
    out = jnp.einsum('bhgqk,bkhd->bqhgd', p, v)
    return out.reshape(B, C, H * D)

def multiscale_pool(u, pool_w, pool_scale):
    B, L, _ = u.shape
    uf = u.astype(jnp.float32)
    csum = jnp.pad(jnp.cumsum(uf, axis=1), ((0, 0), (1, 0), (0, 0)))
    t = jnp.arange(L)
    outs = []
    for g, w in enumerate(POOL_WINDOWS):
        lo = jnp.clip(t - w // 2, 0, L)
        hi = jnp.clip(t - w // 2 + w, 0, L)
        cs = csum[..., g * POOL_GROUP_DIM:(g + 1) * POOL_GROUP_DIM]
        mean = (cs[:, hi] - cs[:, lo]) / (hi - lo).astype(jnp.float32)[None, :, None]
        outs.append(mean - uf[..., g * POOL_GROUP_DIM:(g + 1) * POOL_GROUP_DIM])
    pooled = jnp.stack(outs, axis=2)
    mixed = jnp.einsum('blgc,gcd->blgd', pooled, pool_w.astype(jnp.float32)).reshape(B, L, POOL_WIDTH)
    return (mixed * pool_scale.astype(jnp.float32)).astype(u.dtype)

def squared_relu_mlp(h, w_up, w_down):
    return jnp.square(jax.nn.relu(h @ w_up)) @ w_down

def second_inputs(seed: int = 0) -> dict:
    key = jax.random.key(seed)
    ks = jax.random.split(key, 18)
    f32 = jnp.float32
    nrm = lambda k, shape, s: jax.random.normal(k, shape, f32) * s
    return {
        "x": nrm(ks[0], (BATCH, SEQ, D_MODEL), 1.0),
        "c": nrm(ks[1], (BATCH, D_MODEL), 1.0),
        "ctx": nrm(ks[2], (BATCH, CTX_LEN, D_MODEL), 1.0),
        "c_ctx": nrm(ks[3], (D_MODEL,), 1.0),
        "norm_attn_w": 1.0 + nrm(ks[4], (DEPTH, D_MODEL), 0.02),
        "norm_mlp_w": 1.0 + nrm(ks[5], (DEPTH, D_MODEL), 0.02),
        "w_ada": nrm(ks[6], (DEPTH, D_MODEL, N_MOD * D_MODEL), 0.5 * D_MODEL ** -0.5),
        "b_ada": nrm(ks[7], (DEPTH, N_MOD * D_MODEL), 0.02),
        "w_in": nrm(ks[8], (DEPTH, D_MODEL, IN_WIDTH), D_MODEL ** -0.5),
        "attn_sink": nrm(ks[9], (DEPTH, N_Q_HEADS), 1.0),
        "pool_w": nrm(ks[10], (DEPTH, POOL_GROUPS, POOL_GROUP_DIM, POOL_GROUP_DIM), POOL_GROUP_DIM ** -0.5),
        "pool_scale": 1.0 + nrm(ks[11], (DEPTH, POOL_WIDTH), 0.1),
        "w_out": nrm(ks[12], (DEPTH, MIX_WIDTH, D_MODEL), MIX_WIDTH ** -0.5),
        "w_mlp_up": nrm(ks[13], (DEPTH, D_MODEL, D_FF), D_MODEL ** -0.5),
        "w_mlp_down": nrm(ks[14], (DEPTH, D_FF, D_MODEL), D_FF ** -0.5),
        "final_norm_w": 1.0 + nrm(ks[15], (D_MODEL,), 0.02),
    }

def second_block(x, c, ctx, c_ctx, norm_attn_w, norm_mlp_w, w_ada, b_ada, w_in, attn_sink,
              pool_w, pool_scale, w_out, w_mlp_up, w_mlp_down, final_norm_w):
    seq_len = x.shape[1]
    row, col = axial_positions(seq_len)
    for layer in range(DEPTH):
        sh_a, sc_a, g_a, sh_m, sc_m, g_m = ada_modulation(c, w_ada[layer], b_ada[layer])
        csh_a, csc_a, cg_a, csh_m, csc_m, cg_m = ada_modulation(c_ctx, w_ada[layer], b_ada[layer])

        h = modulate(rms_norm_2(x, norm_attn_w[layer]), sh_a, sc_a)
        hc = modulate(rms_norm_2(ctx, norm_attn_w[layer]), csh_a, csc_a)
        q, k, v, u = split_projection(h @ w_in[layer])
        qc, kc, vc, uc = split_projection(hc @ w_in[layer])
        q = rope_2d(q, row, col)
        k = rope_2d(k, row, col)
        attn = latent_window_attention(q, k, v, kc, vc, attn_sink[layer])
        pool = multiscale_pool(u, pool_w[layer], pool_scale[layer])
        x = x + g_a * (jnp.concatenate([attn, pool], axis=-1) @ w_out[layer])

        hm = modulate(rms_norm_2(x, norm_mlp_w[layer]), sh_m, sc_m)
        x = x + g_m * squared_relu_mlp(hm, w_mlp_up[layer], w_mlp_down[layer])

        if layer < DEPTH - 1:
            attn_c = context_attention(qc, kc, vc, attn_sink[layer])
            pool_c = multiscale_pool(uc, pool_w[layer], pool_scale[layer])
            ctx = ctx + cg_a * (jnp.concatenate([attn_c, pool_c], axis=-1) @ w_out[layer])
            hcm = modulate(rms_norm_2(ctx, norm_mlp_w[layer]), csh_m, csc_m)
            ctx = ctx + cg_m * squared_relu_mlp(hcm, w_mlp_up[layer], w_mlp_down[layer])
    return rms_norm_2(x, final_norm_w)


def setup_inputs(seed=0):
    out = dict(first_inputs(seed))
    for name, value in second_inputs(seed + 1).items():
        if name != "x":
            out[name + "_2"] = value
    return out


def reference(
    x, norm_gain, w_in, conv_w, q_norm_gain, k_norm_gain, conv_out_gain, attn_out_gain, w_out,
    c_2, ctx_2, c_ctx_2, norm_attn_w_2, norm_mlp_w_2, w_ada_2, b_ada_2, w_in_2, attn_sink_2,
    pool_w_2, pool_scale_2, w_out_2, w_mlp_up_2, w_mlp_down_2, final_norm_w_2,
):
    x = first_block(
        x, norm_gain, w_in, conv_w, q_norm_gain, k_norm_gain, conv_out_gain, attn_out_gain,
        w_out,
    )
    return second_block(
        x, c_2, ctx_2, c_ctx_2, norm_attn_w_2, norm_mlp_w_2, w_ada_2, b_ada_2, w_in_2,
        attn_sink_2, pool_w_2, pool_scale_2, w_out_2, w_mlp_up_2, w_mlp_down_2, final_norm_w_2,
    )


_drawn_inputs = setup_inputs


def setup_inputs(seed=0):
    import zlib

    import numpy as np

    out = dict(_drawn_inputs(seed))
    spreads = {}
    factors = {'ctx_2': 4.045,
     'norm_attn_w_2': 8.0,
     'norm_mlp_w_2': 7.36,
     'attn_sink_2': 8.0,
     'pool_scale_2': 3.065,
     'final_norm_w_2': 2.915}
    for name, (base, spread) in spreads.items():
        noise = np.random.default_rng([zlib.crc32(name.encode()), seed]).standard_normal(out[name].shape)
        drawn = base * np.exp(spread * noise) if base else spread * noise
        out[name] = __import__('jax').numpy.asarray(drawn.astype(out[name].dtype))
    for name, factor in factors.items():
        out[name] = (out[name] * factor).astype(out[name].dtype)
    return out
```

```python
from contextlib import ExitStack, contextmanager

import numpy as np

import concourse.bass as bass
from concourse import mybir

ALU = mybir.AluOpType
ACT = mybir.ActivationFunctionType
AX = mybir.AxisListType
F32 = mybir.dt.float32
F32R = mybir.dt.float32r
BF16 = mybir.dt.bfloat16

P = 128
T = 256
D = 2048
KT = D // P
HALF = KT // 2 * P
EPS = 1e-6
HD1 = 128
HD2 = 64
HEADS = 8
CONV_TILES = 8
UNITS_IN, UNITS_OUT = 64, 16
UNITS_KV, UNITS_Q, UNITS_U = 8, 8, 8
MLP_GROUPS = 4
U_OUT1 = UNITS_IN
U_KV = U_OUT1 + UNITS_OUT
U_Q = U_KV + UNITS_KV
U_POOL = U_Q + UNITS_Q
U_OUT2 = U_POOL + UNITS_U
U_MLP = U_OUT2 + UNITS_OUT
UNITS = U_MLP + MLP_GROUPS * 2 * KT
RING = 4
WINDOWS = (2, 4, 8, 16)
PAD = 8
VEC = {}
_at = 0
for _name, _n in (("gain1", 16), ("conv_w", 24), ("conv_gain", 8), ("attn_gain", 8), ("q_gain", 1), ("k_gain", 1),
                  ("norm_attn", 16), ("norm_mlp", 16), ("b_ada", 96), ("pool_scale", 8), ("final", 16),
                  ("c", 16), ("c_ctx", 16)):
    VEC[_name] = _at
    _at += _n
NVEC = _at
ADA_TILES = 96
SH_A, SC_A, G_A, SH_M, SC_M, G_M = range(0, ADA_TILES, KT)


LAPS = {
    "pe heads": {"head": 1, "chunk": 1, "sq": 2, "sum": 2, "norm": 1},
    "pe conv": {"chunk": 1, "sq": 1, "sum": 1},
    "pe w_out": {"chunk": 1},
    "pe q": {"scaled": 8, "rot": 2, "chunk": 1, "values": 2, "tile": 2},
    "act heads": {"half_copied": 4, "hi_done": 8, "head": 1, "probs_ready": 1, "v_copied": 1, "p_copied": 1, "sum": 2, "sq_ready": 2, "chunk": 1, "ada_copied": 1, "head_copied": 1, "z_exp": 1},
    "act conv": {"half_copied": 4, "hi_done": 8, "nt": 1, "nt_hi": 1, "chunk": 1, "ada_copied": 1, "x_new": 1, "sum": 1, "sq_ready": 1, "z_exp": 1},
    "act w_out": {"half_copied": 4, "nt": 4, "nt_hi": 4, "sqs": 4, "x_new": 4, "sq_ready": 4, "hi_done": 8, "chunk": 1, "ada_copied": 1},
    "act q": {"half_copied": 2, "p_turned": 4, "p_copied": 4, "chunk": 1, "ada_copied": 1, "hi_done": 4, "values": 2, "nt_hi": 2, "tile": 2, "es_ready": 2, "probs_ready": 8},
    "act w_out_2": {"half_copied": 4, "sqs": 4, "x_new": 4, "sq_ready": 4, "hi_done": 8},
    "act up": {"half_copied": 2, "nt": 2, "nt_hi": 2, "hi_done": 4},
    "act down": {"half_copied": 2, "hi_done": 4},
    "act last down": {"half_copied": 2, "hi_done": 4, "sqs": 2, "x_new": 2, "sq_ready": 2},
    "dve heads": {"evac_done": 4, "head": 1, "seq": 4, "negmax_ready": 1, "lo_done": 8, "probs_scaled": 1, "sum": 2, "sum_taken": 2, "ms_ready": 1, "norm": 1, "diag_ready": 1, "qk_ready": 1, "z": 1, "chunk": 1, "ada_added": 1},
    "dve conv": {"evac_done": 4, "seq": 7, "nt_ready": 1, "lo_done": 8, "nt": 1, "inB": 1, "x_new": 1, "z": 1, "chunk": 1, "ada_added": 1, "sum": 1, "sum_taken": 1},
    "dve w_out": {"evac_done": 4, "x_new": 4, "seq": 4, "nt_ready": 4, "lo_done": 8, "nt": 4, "inC": 4, "sqs": 4, "sq_added": 4, "chunk": 1, "ada_added": 1},
    "dve q": {"evac_done": 2, "p_turned": 4, "p_copied2": 4, "rot": 2, "seq": 14, "rope_done": 2, "qr_ready": 2, "nt": 2, "inB": 2, "scores": 8, "negmax_ready": 2, "lo_done": 4, "tile": 2, "probs_scaled": 8, "chunk": 1, "ada_added": 1},
    "dve w_out_2": {"evac_done": 4, "x_new": 4, "lo_done": 8, "sqs": 4, "sq_added": 4},
    "dve up": {"evac_done": 2, "nt_ready": 2, "lo_done": 4, "nt": 2, "inB": 2},
    "dve down": {"evac_done": 2, "lo_done": 4},
    "dve last down": {"evac_done": 2, "seq": 2, "x_new": 2, "lo_done": 4, "sqs": 2, "sq_added": 2},
}


class Turns:

    def __init__(self):
        self.base, self.i, self.per, self.local = {}, None, {}, {}

    def value(self, name, back=0):
        v = self.base.get(name, 0) + self.local.get(name, 0) - back
        if self.i is None or not self.per.get(name, 0):
            return v
        return self.i * self.per[name] + v

    def next(self, name, back=0):
        self.local[name] = self.local.get(name, 0) + 1
        return self.value(name, back)

    def _close(self):
        for name, n in self.local.items():
            self.base[name] = self.base.get(name, 0) + n
        self.local = {}

    @contextmanager
    def lap(self, eng, n, name):
        self._close()
        per = LAPS.get(name, {})
        with eng.Fori(0, n) as i:
            self.i, self.per = i, per
            yield i
        assert self.local == per, (name, self.local)
        for name, count in per.items():
            self.base[name] = self.base.get(name, 0) + n * count
        self.i, self.per, self.local = None, {}, {}


def program(nc, t_in, out):
    with ExitStack() as ctx:
        def sb(name, shape, dt=F32):
            return ctx.enter_context(nc.sbuf_tensor(name, shape, dt))

        def sem(name):
            return ctx.enter_context(nc.semaphore(name))

        resid = sb("resid", [P, KT, T])
        actA = sb("actA", [P, KT, 2 * T], F32R)
        actB = sb("actB", [P, KT, 2 * T], F32R)
        raw = sb("raw", [P, RING, HALF])
        hi = sb("hi", [P, RING, HALF], F32R)
        lo = sb("lo", [P, RING, HALF], F32R)
        ada_raw = sb("ada_raw", [P, 2, 4, 512])
        vec = sb("vec", [P, NVEC])
        adav = sb("adav", [P, 2, ADA_TILES])
        scale_a = sb("scale_a", [P, 2, KT])
        scale_m = sb("scale_m", [P, KT])
        ident = sb("ident", [P, P])
        ones = sb("ones", [P, P])
        sel = sb("sel", [P, 2])
        cpad = sb("cpad", [P, KT, 32])
        maskb = sb("maskb", [P, 4, P], BF16)
        sinks = sb("sinks", [P, 32])
        ss = sb("ss", [P, 12])
        ms = sb("ms", [P, 4])
        rr = sb("rr", [P, 4])
        neg_half = sb("neg_half", [P, 4])
        sqsum = sb("sqsum", [P, T])
        tmpB = sb("tmpB", [P, 2, T])
        t4 = sb("t4", [P, 4, T])
        sq = sb("sq", [P, 2, T])
        sm = sb("sm", [P, 48])
        W = sb("W", [P, 4096])
        diag, adas = W[:, 3328:3584], W[:, 3584:4096]
        ctx_raw = W[:, 0:1024].rearrange("p (s t) -> p s t", s=4)
        yq, yk, yv, yz = (W[:, i * T:(i + 1) * T] for i in range(4))
        qg, kn, ze = (W[:, i * T:(i + 1) * T] for i in range(4, 7))
        Vt1 = W[:, 1792:2048]
        P1 = W[:, 2048:2432]
        PT1 = W[:, 2432:2816]
        upad = W[:, 2816:2816 + 2 + T]
        cw = W[:, 3080:3083]
        kT = W[:, 0:512].rearrange("p (m t) -> p m t", m=2)
        kcT = W[:, 512:1024].rearrange("p (m t) -> p m t", m=2)
        V2 = W[:, 1024:1536].rearrange("p (t n) -> p t n", t=2)
        Vc = W[:, 1536:2048].rearrange("p (t n) -> p t n", t=2)
        y2 = W[:, 2048:2560].rearrange("p (s t) -> p s t", s=2)
        qr = W[:, 2560:2816]
        t2a, t2b = W[:, 2816:3072], W[:, 3072:3328]
        with nc.sbuf_tensor("x_tok", [P, 2, D], F32) as x_tok, nc.sbuf_tensor("ctx_tok", [P, 2, D], F32) as ctx_tok:
            pass
        with nc.sbuf_tensor("mix1", [P, 4, 8, T], F32) as mix1:
            pass
        y_attn, z_attn, y_conv, z_conv = (mix1[:, i] for i in range(4))
        with nc.sbuf_tensor("actC", [P, KT, 2 * T], F32R) as actC:
            pass
        with nc.sbuf_tensor("blk2", [P, 8192], F32) as blk2:
            pass
        probs = blk2[:, 0:2048].rearrange("p (c n) -> p c n", c=4)
        turned = blk2[:, 2048:4096].rearrange("p (h k t) -> p h k t", h=2, k=4)
        upad2 = blk2[:, 4096:4096 + 2 * 272].rearrange("p (s n) -> p s n", s=2)
        wsA = blk2[:, 4640:4640 + 272]
        wsB = blk2[:, 4912:4912 + 272]
        pooled = blk2[:, 5184:5696].rearrange("p (s t) -> p s t", s=2)
        inv_count = blk2[:, 5696:6720].rearrange("p (g t) -> p g t", g=4)
        rope = blk2[:, 6720:7232].rearrange("p (s t) -> p s t", s=2)
        rot = blk2[:, 7232:7360]
        acc = sb("acc", [P, 8192])[:, 0:4096].rearrange("p (k t) -> p k t", k=KT)
        pool_w = ada_raw[:, 0].rearrange("p k n -> p (k n)").rearrange("p (g k n) -> p g k n", g=4, k=2)
        G = [ctx.enter_context(nc.psum_tensor(f"G{i}", [P, 512], F32)) for i in range(2)]
        ADA = ctx.enter_context(nc.psum_tensor("ADA", [P, 512], F32))
        M = ctx.enter_context(nc.psum_tensor("M", [P, 512], F32))
        S = [ctx.enter_context(nc.psum_tensor(f"S{i}", [P, 512], F32)) for i in range(4)]
        BC = M[:, 0:T]
        SUMS = S[1][:, 3 * P:3 * P + 4]
        ROT = M[:, T:2 * T]
        CTX_BC = S[3][:, T:2 * T]

        ORDER = (0, 2, 1, 3)

        small_in = sem("small_in")
        tok_in, ctxtok_in, resid_in, pool_in, blk2_in = (
            sem(n) for n in ("tok_in", "ctxtok_in", "resid_in", "pool_in", "blk2_in"))
        raw_full = [sem(f"raw_full{i}") for i in range(RING)]
        ada_full = [sem(f"ada_full{i}") for i in range(2)]
        ctx_full = [sem(f"ctx_full{i}") for i in range(4)]
        hi_done = sem("hi_done")
        lo_done = sem("lo_done")
        w_used = sem("w_used")
        half_copied = sem("half_copied")
        evac_done = sem("evac_done")
        ada_used = sem("ada_used")
        ada_copied = sem("ada_copied")
        ada_summed = sem("ada_summed")
        ada_added = sem("ada_added")
        sq_ready = sem("sq_ready")
        sum_ready = sem("sum_ready")
        sum_taken = sem("sum_taken")
        sq_added = sem("sq_added")
        x_new = sem("x_new")
        c_exp, es_ready = sem("c_exp"), sem("es_ready")
        ms_ready = sem("ms_ready")
        rstd_ready = sem("rstd_ready")
        diag_ready = sem("diag_ready")
        bc_ready = sem("bc_ready")
        nt_ready = sem("nt_ready")
        nt_hi = sem("nt_hi")
        inA, inB, inC = sem("inA"), sem("inB"), sem("inC")
        c_ready, scale_ready = sem("c_ready"), sem("scale_ready")
        const_ready = sem("const_ready")
        scores_ready, negmax_ready, probs_ready, probs_scaled = (sem(n) for n in (
            "scores_ready", "negmax_ready", "probs_ready", "probs_scaled"))
        v_turned, v_copied, p_turned, p_copied, p_copied2 = (sem(n) for n in (
            "v_turned", "v_copied", "p_turned", "p_copied", "p_copied2"))
        head_ready, head_copied = sem("head_ready"), sem("head_copied")
        qk_ready, z_exp = sem("qk_ready"), sem("z_exp")
        qr_ready = sem("qr_ready")
        rot_ready, rope_done = sem("rot_ready"), sem("rope_done")
        pooled_ready, pool_ready = sem("pooled_ready"), sem("pool_ready")
        sink_ready, acc_zero = sem("sink_ready"), sem("acc_zero")
        out_ready, out_sent = sem("out_ready"), sem("out_sent")
        dve_seq, act_seq = sem("dve_seq"), sem("act_seq")

        block = ctx.enter_context(nc.Block())

        @block.sync
        def _(sp):
            stream, ada_w = t_in["stream"], t_in["w_ada"]

            def weight(slot, n, first=False):
                row = n if isinstance(n, int) else sp.snap(n)
                if not first:
                    free = n - 3 if isinstance(n, int) else sp.snap(n - 3)
                    sp.wait_ge(lo_done, free)
                src = stream[row] if isinstance(row, int) else stream[bass.ds(row, 1)].rearrange("a p n -> (a p) n")
                sp.dma_start(raw[:, slot, :], src).then_inc(raw_full[slot], 16)

            def ada(n, slot, first=False):
                row = n if isinstance(n, int) else sp.snap(n)
                if not first:
                    free = n - 1 if isinstance(n, int) else sp.snap(n - 1)
                    sp.wait_ge(ada_used, free)
                src = ada_w[row] if isinstance(row, int) else ada_w[bass.ds(row, 1)].rearrange("a p n -> (a p) n")
                sp.dma_start(ada_raw[:, slot].rearrange("p k n -> p (k n)"), src).then_inc(ada_full[slot], 16)

            sp.dma_start(x_tok[:], t_in["x_tok"]).then_inc(tok_in, 16)
            for dst, name in ((vec, "vec"), (ident, "ident"), (ones, "ones"), (sel, "sel"), (sinks, "sinks")):
                sp.dma_start(dst[:], t_in[name]).then_inc(small_in, 16)
            sp.dma_start(maskb[:], t_in["masks"]).then_inc(small_in, 16)
            sp.dma_start(resid[:], t_in["xT"]).then_inc(resid_in, 16)
            for s in range(RING):
                weight(s, s, first=True)
            sp.dma_start(ctx_tok[:], t_in["ctx_tok"]).then_inc(ctxtok_in, 16)

            for n in range(RING, 2 * RING):
                weight(n % RING, n)
            ada(0, 0, first=True)
            ada(1, 1, first=True)
            with sp.Fori(0, U_KV // 4) as i:
                for j in range(4):
                    ada(i * 4 + j + 2, j % 2)
                    weight(2 * j % RING, i * 8 + 2 * j + 8)
                    weight((2 * j + 1) % RING, i * 8 + 2 * j + 9)
            with sp.Fori(0, UNITS_KV * 2 // RING) as i:
                for j in range(RING):
                    weight(j, i * RING + 2 * U_KV + 8 + j)

            def q_lap(i, more):
                ada(i * 4 + 82, 0)
                ada(i * 4 + 83, 1)
                weight(0, i * 4 + 2 * U_Q + 8)
                weight(1, i * 4 + 2 * U_Q + 9)
                if more:
                    ada(i * 4 + 84, 0)
                    ada(i * 4 + 85, 1)
                weight(2, i * 4 + 2 * U_Q + 10)
                weight(3, i * 4 + 2 * U_Q + 11)

            with sp.Fori(0, 3) as i:
                q_lap(i, True)
            q_lap(3, False)
            with sp.Fori(0, (2 * UNITS - 2 * U_POOL - 8) // RING) as i:
                for j in range(RING):
                    weight(j, i * RING + 2 * U_POOL + 8 + j)
            for i in range(4):
                sp.wait_ge(out_ready, 4 * i + 4)
                sp.dma_start(out[:, 4 * i:4 * i + 4, :], resid[:, 4 * i:4 * i + 4, :]).then_inc(out_sent, 16)
            sp.wait_ge(out_sent, 64)


        class At:

            def __init__(self, base, per=0, i=0):
                self.base, self.per, self.i = base, per, i

            def unit(self, j, add=0, times=1):
                v = (self.base + j) * times + add
                return v if isinstance(self.i, int) and not self.i else self.i * (self.per * times) + v

            def loads(self, j, half):
                v = self.base // 2 + 2 + (2 * j + half) // 4
                return v if isinstance(self.i, int) and not self.i else self.i * (self.per // 2) + v

        @block.gpsimd
        def _(pool):
            pool.memset(neg_half[:], -0.5).then_inc(const_ready, 1)
            pool.memset(ms[:], 1.0).then_inc(const_ready, 1)
            pool.memset(ss[:], 0.0).then_inc(const_ready, 1)
            for t in range(2):
                pool.memset(sqsum[:, t * P:(t + 1) * P], 0.0).then_inc(sq_added, 1)
            pool.wait_ge(sq_added, 2)
            pool.memset(W[:, 2816:2818], 0.0).then_inc(const_ready, 1)
            pool.memset(cpad[:], 0.0).then_inc(const_ready, 1)
            pool.wait_ge(const_ready, 5)

            def power(n):
                pool.wait_ge(ms_ready, n)
                pool.tensor_tensor(rr[:], ms[:], neg_half[:], ALU.pow).then_inc(rstd_ready, 1)

            with pool.Fori(0, 12) as i:
                power(i + 1)
            pool.wait_ge(inB, 16)
            for s in range(4):
                pool.dma_start(ctx_raw[:, s], t_in["ctxT"][:, s]).then_inc(ctx_full[s], 16)
            with pool.Fori(0, 3) as i:
                for s in range(4):
                    pool.wait_ge(inC, i * 4 + s + 1)
                    pool.dma_start(ctx_raw[:, s:s + 1], t_in["ctxT"][:, bass.ds(i * 4 + 4 + s, 1)]).then_inc(ctx_full[s], 16)
            power(13)
            pool.wait_ge(w_used, 2 * U_KV + 8)
            pool.dma_start(inv_count, t_in["inv_count"]).then_inc(blk2_in, 16)
            pool.dma_start(rope, t_in["rope"]).then_inc(blk2_in, 16)
            pool.dma_start(rot, t_in["rot"]).then_inc(blk2_in, 16)
            pool.memset(upad2, 0.0).then_inc(sink_ready, 1)
            pool.wait_ge(ada_used, 96)
            pool.dma_start(pool_w, t_in["pool_w"]).then_inc(pool_in, 16)
            power(14)
            pool.memset(acc, 0.0).then_inc(acc_zero, 1)
            power(15)

        @block.tensor
        def _(pe):
            turn = Turns()

            def half_unit(at, j, half, x, ready=None, ready_base=0):
                slot = (2 * j + half) % RING
                pe.wait_ge(lo_done, at.unit(j, 1 + half, 2))
                if half == 0 and not (isinstance(at.i, int) and at.base + j < 2):
                    pe.wait_ge(evac_done, at.unit(j, -1))
                bank = G[j % 2]
                for n in range(KT // 2):
                    k = half * KT // 2 + n
                    if ready is not None:
                        pe.wait_ge(ready, ready_base + k + 1)
                    cols = slice(n * P, (n + 1) * P)
                    pe.matmul(bank[:], hi[:, slot, cols], x[:, k, :], start=(k == 0), stop=False, skip_group_check=True)
                    m = pe.matmul(bank[:, 0:T], lo[:, slot, cols], x[:, k, 0:T], start=False, stop=(k == KT - 1),
                                  skip_group_check=True)
                m.then_inc(w_used, 1)

            def unit(at, j, x, ready=None, ready_base=0, ada=None):
                half_unit(at, j, 0, x, ready, ready_base)
                if ada is not None:
                    ada_rows(ada)
                half_unit(at, j, 1, x, ready, ready_base)

            def ada_rows(q):
                c = turn.value("chunk")
                if q == 0:
                    if isinstance(c, int) and c == 0:
                        pe.wait_ge(c_ready, 2)
                    else:
                        pe.wait_ge(ada_added, c)
                pe.wait_ge(ada_full[q % 2], c * 32 + 16 * (q // 2 + 1))
                for g in range(4):
                    m = pe.matmul(ADA[32 * g:32 * g + 32, :], cpad[:, 4 * q + g, :], ada_raw[:, q % 2, g, :],
                                  start=(q == 0), stop=(q == 3), tile_position=(0, 32 * g), skip_group_check=True)
                m.then_inc(ada_used, 1)
                if q == 3:
                    turn.next("chunk")

            def ada_turn():
                pe.wait_ge(ada_copied, turn.value("chunk"))
                for m in range(4):
                    x = pe.matmul(ADA[:, 2 * m:2 * m + 2], adas[:, m * P:(m + 1) * P], sel[:], start=(m == 0), stop=(m == 3),
                                  skip_group_check=True)
                x.then_inc(ada_summed, 1)

            def token_sums(tiles, wait_sq=True):
                if wait_sq:
                    pe.wait_ge(sq_ready, turn.next("sq"))
                n = turn.next("sum", 1)
                if not (isinstance(n, int) and n == 0):
                    pe.wait_ge(sum_taken, n)
                for c, x in enumerate(tiles):
                    m = pe.matmul(SUMS[:, c:c + 1], x, ones[:, 0:1], start=(c == 0), stop=(c == len(tiles) - 1),
                                  skip_group_check=True)
                m.then_inc(sum_ready, 1)

            def broadcast(dst=BC):
                pe.wait_ge(diag_ready, turn.next("norm"))
                pe.matmul(dst, ones[:], diag, start=True, stop=True, skip_group_check=True).then_inc(bc_ready, 1)

            def head_scores():
                pe.wait_ge(qk_ready, turn.next("head"))
                pe.matmul(S[0][:, 0:P], qg[:, 0:P], kn[:, 0:P], start=True, stop=False, skip_group_check=True)
                pe.matmul(S[0][:, 0:P], maskb[:, 0], maskb[:, 1], start=False, stop=False, skip_group_check=True)
                pe.matmul(S[0][:, P:3 * P], qg[:, P:T], kn[:], start=False, stop=False, skip_group_check=True)
                pe.matmul(S[0][:, T:3 * P], maskb[:, 0], maskb[:, 1], start=False, stop=True,
                          skip_group_check=True).then_inc(scores_ready, 1)
                pe.transpose(S[2][:, 0:P], yv[:, 0:P], ident[:])
                pe.transpose(S[2][:, P:T], yv[:, P:T], ident[:]).then_inc(v_turned, 1)

            def head_turn():
                pe.wait_ge(probs_scaled, turn.value("head"))
                for n in range(3):
                    m = pe.transpose(S[1][:, n * P:(n + 1) * P], P1[:, n * P:(n + 1) * P], ident[:])
                m.then_inc(p_turned, 1)

            def head_values():
                pe.wait_ge(p_copied, turn.value("head"))
                pe.wait_ge(v_copied, turn.value("head"))
                pe.matmul(S[3][:, 0:T], Vt1[:, 0:P], PT1[:, 0:T], start=True, stop=False, skip_group_check=True)
                pe.matmul(S[3][:, P:T], Vt1[:, P:T], PT1[:, T:3 * P], start=False, stop=True,
                          skip_group_check=True).then_inc(head_ready, 1)

            ss0 = [sq[:, 0, 0:P], sq[:, 0, P:T]]
            ss1 = [sq[:, 1, 0:P], sq[:, 1, P:T]]
            ssum = [sqsum[:, 0:P], sqsum[:, P:T]]

            def head_body(at, prev, first):
                unit(at, 0, actA, inA if first else None, ada=0)
                if prev:
                    head_scores()
                unit(at, 1, actA, ada=1)
                if prev:
                    head_turn()
                unit(at, 2, actA, ada=2)
                if prev:
                    head_values()
                token_sums(ss0 + ss1)
                unit(at, 3, actA, ada=3)
                ada_turn()
                broadcast()
                if prev:
                    token_sums(ss0)

            def conv_body(at, tail):
                unit(at, 0, actA, ada=0)
                if tail:
                    head_scores()
                unit(at, 1, actA, ada=1)
                if tail:
                    head_turn()
                unit(at, 2, actA, ada=2)
                if tail:
                    head_values()
                unit(at, 3, actA, ada=3)
                if tail:
                    token_sums(ss0)
                ada_turn()
                token_sums(ss1)
                if tail:
                    broadcast()

            pe.wait_ge(small_in, 96)
            broadcast()
            head_body(At(0), False, True)
            broadcast(CTX_BC)
            with turn.lap(pe, 7, "pe heads") as i:
                head_body(At(4, 4, i), True, False)
            conv_body(At(32), True)
            with turn.lap(pe, 7, "pe conv") as i:
                conv_body(At(36, 4, i), False)
            broadcast()
            with turn.lap(pe, 4, "pe w_out") as i:
                at = At(U_OUT1, 4, i)
                for j in range(4):
                    unit(at, j, actB, inB, ada=j)
                    if j == 3:
                        ada_turn()

            def total_sums(n):
                pe.wait_ge(sq_added, 2 + 16 * n)
                turn.base["sq"] = turn.value("sq") + 16
                token_sums(ssum, wait_sq=False)

            def turn_values(y, evacuated, copied):
                pe.wait_ge(evac_done, evacuated)
                pe.wait_ge(v_copied, copied)
                pe.transpose(S[2][:, 0:P], y[:, 0:P], ident[:])
                pe.transpose(S[2][:, P:T], y[:, P:T], ident[:]).then_inc(v_turned, 1)

            def rotate(y, evacuated):
                pe.wait_ge(evac_done, evacuated)
                n = turn.next("rot", 1)
                if not (isinstance(n, int) and n == 0):
                    pe.wait_ge(rope_done, n)
                pe.matmul(ROT, rot, y, start=True, stop=True, skip_group_check=True).then_inc(rot_ready, 1)

            at = At(U_KV)
            unit(at, 0, actC, inC)
            total_sums(1)
            half_unit(at, 1, 0, actC)
            broadcast()
            half_unit(at, 1, 1, actC)
            unit(at, 2, actC)
            unit(at, 3, actC)
            turn_values(y2[:, 0], U_KV + 3, 8)
            unit(at, 4, actA, inA, KT)
            turn_values(y2[:, 1], U_KV + 4, 9)
            unit(at, 5, actA)
            pe.wait_ge(blk2_in, 48)
            rotate(y2[:, 0], U_KV + 5)
            unit(at, 6, actA)
            rotate(y2[:, 1], U_KV + 6)
            unit(at, 7, actA)
            turn_values(y2[:, 0], U_KV + 7, 10)

            def tile_scores(s):
                pe.wait_ge(qr_ready, turn.next("tile"))
                for t in range(2):
                    for h in range(2):
                        rows = slice(64 * h, 64 * h + 64)
                        bank = S[2 * h + t]
                        q = qr[rows, t * P:(t + 1) * P]
                        pe.matmul(bank[:, 0:T], q, kT[rows, s, :], start=True, stop=False, skip_group_check=True)
                        pe.matmul(bank[:, T:2 * T], q, kcT[rows, s, :], start=False, stop=False, skip_group_check=True)
                for t in range(2):
                    for h in range(2):
                        cols = slice(P, T) if t == 0 else slice(0, P)
                        pe.matmul(S[2 * h + t][:, cols], maskb[:, 0], maskb[:, 2 + t], start=False, stop=True,
                                  skip_group_check=True).then_inc(scores_ready, 1)

            def tile_turn():
                for c in ORDER:
                    pe.wait_ge(probs_scaled, turn.next("scaled"))
                    for k in range(4):
                        m = pe.transpose(S[c][:, k * P:(k + 1) * P], probs[:, c, k * P:(k + 1) * P], ident[:])
                    m.then_inc(p_turned, 1)

            def tile_values(s):
                n = turn.next("values")
                pe.wait_ge(p_copied, n * 2 + HEADS)
                pe.wait_ge(p_copied2, n * 2)
                pe.wait_ge(inB, n + (KT - 1))
                pe.wait_ge(rope_done, turn.value("rot"))
                for k in range(4):
                    v = V2 if k < 2 else Vc
                    for h in range(2):
                        g = 128 * s + 64 * h
                        m = pe.matmul(M[64 * h:64 * h + 64, 0:T], v[:, k % 2, g:g + 64], turned[:, h, k, :],
                                      start=(k == 0), stop=(k == 3), tile_position=(0, 64 * h), skip_group_check=True)
                m.then_inc(head_ready, 1)

            def slot(at, s, before, last, ada=False):
                unit(at, s, actA)
                if before:
                    tile_turn()
                if last:
                    if before:
                        pe.wait_ge(inB, turn.value("values") + KT)
                    rotate(y2[:, 1 - s], at.unit(s))
                if ada:
                    ada_rows(2 * s)
                    ada_rows(2 * s + 1)
                if before:
                    tile_values(s)
                if last:
                    tile_scores(1 - s)
                if ada and s == 1:
                    ada_turn()

            turn.base["scaled"] = HEADS
            at = At(U_Q)
            unit(at, 0, actA)
            turn_values(y2[:, 1], U_KV + 8, 11)
            ada_rows(0)
            ada_rows(1)
            unit(at, 1, actA)
            rotate(y2[:, 0], U_Q + 1)
            ada_rows(2)
            ada_rows(3)
            pe.wait_ge(v_copied, 12)
            tile_scores(0)
            ada_turn()
            with turn.lap(pe, 3, "pe q") as i:
                at = At(U_Q + 2, 2, i)
                slot(at, 0, True, True, ada=True)
                slot(at, 1, True, True, ada=True)
            at = At(U_POOL)
            slot(at, 0, True, True)
            slot(at, 1, True, False)

            def mix(g):
                pe.wait_ge(pooled_ready, g + 1)
                if g == 0:
                    pe.wait_ge(pool_in, 16)
                else:
                    pe.wait_ge(inB, KT + 8 + 2 * g)
                for m in range(2):
                    for k in range(2):
                        x = pe.matmul(S[m][:, 0:T], pool_w[:, g, k, m * P:(m + 1) * P], pooled[:, k, :],
                                      start=(k == 0), stop=(k == 1), skip_group_check=True)
                x.then_inc(pool_ready, 1)

            for n in range(2, UNITS_U):
                unit(at, n, actA)
                if n % 2 == 0:
                    mix(n // 2 - 1)
            at = At(U_OUT2)
            pe.wait_ge(inB, KT + 8)
            half_unit(at, 0, 0, actB)
            mix(3)
            half_unit(at, 0, 1, actB, inB, KT)
            unit(at, 1, actB)
            with turn.lap(pe, (UNITS_OUT - 2) // 2, "pe w_out_2") as i:
                for j in range(2):
                    unit(At(U_OUT2 + 2, 2, i), j, actB)
            total_sums(2)
            broadcast()

            def pair_units(laps, base, x, ready=None, ready_base=0):
                with turn.lap(pe, laps, "pe mlp") as i:
                    for j in range(2):
                        unit(At(base, 2, i), j, x, ready, ready_base)

            for g in range(MLP_GROUPS):
                base = U_MLP + 2 * KT * g
                pair_units(8, base, actA, inA if g == 0 else None, 2 * KT)
                unit(At(base + KT), 0, actB, inB, KT * (2 + g))
                unit(At(base + KT), 1, actB)
                pair_units(7, base + KT + 2, actB)
            total_sums(3)
            broadcast()

        @block.scalar
        def _(act):
            turn = Turns()

            def own(event):
                act.wait_ge(event, turn.next(event.name))

            def copy(dst, src):
                return act.activation(dst, src, ACT.Copy)

            def split(at, j, half=1):
                slot = (2 * j + half) % RING
                act.wait_ge(raw_full[slot], at.loads(j, half) * 16)
                act.wait_ge(w_used, at.unit(j, 1 + half, 2))
                copy(hi[:, slot], raw[:, slot]).then_inc(hi_done, 1)
                own(hi_done)

            def second_sum(at, j, splits=True, ada=False):
                if splits:
                    split(at, j, 0)
                if ada:
                    ada_copy()
                act.wait_ge(w_used, at.unit(j, 2, 2))
                if not (isinstance(at.i, int) and at.base + j < 2):
                    act.wait_ge(evac_done, at.unit(j, -1))
                copy(tmpB[:, j % 2], G[j % 2][:, T:2 * T]).then_inc(half_copied, 1)
                own(half_copied)

            def evacuated(at, j):
                act.wait_ge(evac_done, at.unit(j, 1))

            def ada_copy():
                n = turn.next("chunk")
                act.wait_ge(ada_used, n * 4)
                copy(adas, ADA[:]).then_inc(ada_copied, 1)
                own(ada_copied)

            def high(dst, src):
                act.wait_ge(nt_ready, turn.next("nt"))
                copy(dst, src).then_inc(nt_hi, 1)
                own(nt_hi)

            def head_probs():
                act.wait_ge(negmax_ready, turn.next("head"))
                act.activation(P1[:, 0:P], S[0][:, 0:P], ACT.Exp, bias=sm[:, 2:3], scale=sm[:, 4:5], accum_out=sm[:, 6:7])
                act.activation(P1[:, P:3 * P], S[0][:, P:3 * P], ACT.Exp, bias=sm[:, 3:4], scale=sm[:, 5:6],
                               accum_out=sm[:, 7:8]).then_inc(probs_ready, 1)
                own(probs_ready)

            def head_copies():
                act.wait_ge(v_turned, turn.value("head"))
                copy(Vt1, S[2][:, 0:T]).then_inc(v_copied, 1)
                own(v_copied)
                act.wait_ge(p_turned, turn.value("head"))
                copy(PT1, S[1][:, 0:3 * P]).then_inc(p_copied, 1)
                own(p_copied)

            def sums_used():
                n = turn.value("sum")
                if not (isinstance(n, int) and n == 0):
                    act.wait_ge(sum_ready, n)
                turn.next("sum")

            def head_out(dst):
                act.wait_ge(head_ready, turn.value("head"))
                copy(dst, S[3][:, 0:T].rearrange("p (a t) -> p a t", a=1)).then_inc(head_copied, 1)
                own(head_copied)
                sums_used()
                act.activation(sq[:, 0], S[3][:, 0:T], ACT.Square).then_inc(sq_ready, 1)
                own(sq_ready)

            def head_body(at, prev):
                second_sum(at, 0)
                split(at, 0)
                if prev is not None:
                    head_probs()
                second_sum(at, 1)
                split(at, 1)
                if prev is not None:
                    head_copies()
                evacuated(at, 1)
                sums_used()
                act.activation(sq[:, 0], yq, ACT.Square)
                act.activation(sq[:, 1], yk, ACT.Square).then_inc(sq_ready, 1)
                own(sq_ready)
                second_sum(at, 2)
                split(at, 2)
                if prev is not None:
                    head_out(prev)
                second_sum(at, 3, ada=True)
                split(at, 3)
                evacuated(at, 3)
                act.activation(ze, yz, ACT.Exp, scale=-1.0).then_inc(z_exp, 1)
                own(z_exp)

            def conv_body(at, tail, i):
                y = y_conv[:, 0:1] if tail else y_conv[:, bass.ds(i + 1, 1)]
                second_sum(at, 0)
                split(at, 0)
                if tail:
                    head_probs()
                if i is not None:
                    high(actB[:, bass.ds(i, 1), 0:T], t4[:, 1:2])
                second_sum(at, 1)
                split(at, 1)
                if tail:
                    head_copies()
                second_sum(at, 2)
                split(at, 2)
                if tail:
                    head_out(y_attn[:, HEADS - 1:HEADS])
                act.wait_ge(x_new, turn.next("x_new"))
                sums_used()
                act.activation(sq[:, 1:2], y, ACT.Square).then_inc(sq_ready, 1)
                own(sq_ready)
                second_sum(at, 3, ada=True)
                split(at, 3)
                evacuated(at, 3)
                act.activation(ze, yz, ACT.Exp, scale=-1.0).then_inc(z_exp, 1)
                own(z_exp)

            act.wait_ge(const_ready, 5)
            act.wait_ge(tok_in, 16)
            for t in range(2):
                act.activation(W[:, 0:D], x_tok[:, t], ACT.Square, accum_out=ss[:, t:t + 1]).then_inc(act_seq, 1)
                act.wait_ge(act_seq, turn.next("seq"))
            act.wait_ge(small_in, 96)
            for n in range(RING):
                act.wait_ge(raw_full[n], 16)
                copy(hi[:, n], raw[:, n]).then_inc(hi_done, 1)
                own(hi_done)
            cc = VEC["c"]
            act.activation(sm[:, 0:32], vec[:, cc:cc + 32], ACT.Exp, scale=-1.0).then_inc(c_exp, 1)
            own(c_exp)
            for k in range(KT):
                high(actA[:, k, 0:T], t4[:, k % 4])
            act.wait_ge(ctxtok_in, 16)
            for t in range(2):
                act.activation(W[:, 0:D], ctx_tok[:, t], ACT.Square, accum_out=ss[:, 2 + t:3 + t]).then_inc(act_seq, 1)
                act.wait_ge(act_seq, turn.next("seq"))

            head_body(At(0), None)
            with turn.lap(act, 7, "act heads") as i:
                head_body(At(4, 4, i), y_attn[:, bass.ds(i, 1)])
            conv_body(At(32), True, None)
            with turn.lap(act, 7, "act conv") as i:
                conv_body(At(36, 4, i), False, i)
            high(actB[:, 7, 0:T], t4[:, 1])
            for k in range(8):
                high(actB[:, 8 + k, 0:T], t4[:, 1 + k % 2])

            def square(src):
                n = turn.next("sqs")
                act.wait_ge(x_new, turn.next("x_new"))
                act.wait_ge(sq_added, n)
                act.activation(src[0], src[1], ACT.Square).then_inc(sq_ready, 1)
                own(sq_ready)

            def out_body(at, i, ctx_too):
                for j in range(4):
                    u = bass.ds(i * 4 + j, 1)
                    second_sum(at, j, ada=ctx_too and j == 3)
                    if ctx_too:
                        high(actC[:, u, 0:T], t4[:, 3:4])
                    square((sq[:, j % 2:j % 2 + 1], resid[:, u]))
                    split(at, j)

            with turn.lap(act, 4, "act w_out") as i:
                out_body(At(U_OUT1, 4, i), i, True)

            def value_copy(dst, count):
                act.wait_ge(v_turned, count)
                copy(dst, S[2][:, 0:T].rearrange("p (t n) -> p t n", t=2)).then_inc(v_copied, 1)
                own(v_copied)

            at = At(U_KV)
            for n in range(UNITS_KV):
                second_sum(at, n)
                split(at, n)
                if n < 4:
                    for k in range(4 * n, 4 * n + 4):
                        high(actA[:, k, 0:T], t4[:, k % 4])
                if n == 3:
                    value_copy(Vc[:, :, 0:P], 9)
                if n == 4:
                    value_copy(Vc[:, :, P:T], 10)
                if n == 7:
                    value_copy(V2[:, :, 0:P], 11)

            def turned_copy(back):
                act.wait_ge(p_turned, turn.next("p_turned", 1) * 2 + HEADS + 1)
                c = back
                copy(turned[:, 0, :, c * P:(c + 1) * P],
                     S[c][:].rearrange("p (k t) -> p k t", k=4)).then_inc(p_copied, 1)
                own(p_copied)

            def slot(at, s, before, last, out_tile=None, ada=False):
                second_sum(at, s)
                if before:
                    turned_copy(0)
                    turned_copy(1)
                if ada and s == 1:
                    ada_copy()
                split(at, s)
                if before:
                    act.wait_ge(head_ready, turn.next("values"))
                    copy(actB[:, out_tile, 0:T], M[:, 0:T].rearrange("p (a t) -> p a t", a=1)).then_inc(nt_hi, 1)
                    own(nt_hi)
                if last:
                    act.wait_ge(negmax_ready, turn.next("tile"))
                    act.activation(sm[:, 16:20], sm[:, 12:16], ACT.Exp).then_inc(es_ready, 1)
                    own(es_ready)
                    for c in ORDER:
                        act.activation(probs[:, c], S[c][:], ACT.Exp, bias=sm[:, 8 + c:9 + c], scale=HD2 ** -0.5,
                                       accum_out=sm[:, 20 + c:21 + c]).then_inc(probs_ready, 1)
                        own(probs_ready)

            turn.base["values"] = HEADS
            turn.base["tile"] = HEADS
            at = At(U_Q)
            second_sum(at, 0)
            value_copy(V2[:, :, P:T], 12)
            split(at, 0)
            slot(at, 1, False, True, ada=True)
            with turn.lap(act, 3, "act q") as i:
                at = At(U_Q + 2, 2, i)
                slot(at, 0, True, True, bass.ds(i, 1), ada=True)
                slot(at, 1, True, True, bass.ds(i + 4, 1), ada=True)
            at = At(U_POOL)
            slot(at, 0, True, True, slice(3, 4))
            slot(at, 1, True, False, slice(7, 8))

            def pool_high(g):
                for m in range(2):
                    high(actB[:, 8 + 2 * g + m, 0:T], t4[:, m])

            for n in range(2, UNITS_U):
                second_sum(at, n)
                split(at, n)
                if n % 2 == 0:
                    pool_high(n // 2 - 1)
            pool_high(3)
            with turn.lap(act, 4, "act w_out_2") as i:
                out_body(At(U_OUT2, 4, i), i, False)
            for k in range(KT):
                high(actA[:, k, 0:T], t4[:, k % 4])

            for g in range(MLP_GROUPS):
                base = U_MLP + 2 * KT * g
                with turn.lap(act, 8, "act up") as i:
                    for j in range(2):
                        second_sum(At(base, 2, i), j)
                        high(actB[:, bass.ds(i * 2 + j, 1), 0:T], t4[:, 2 + j:3 + j])
                        split(At(base, 2, i), j)
                last = g == MLP_GROUPS - 1
                with turn.lap(act, 7 if last else 8, "act last down" if last else "act down") as i:
                    for j in range(2):
                        second_sum(At(base + KT, 2, i), j)
                        split(At(base + KT, 2, i), j)
                        if last:
                            square((sq[:, j:j + 1], resid[:, bass.ds(i * 2 + j, 1)]))
            for j in range(2):
                second_sum(At(UNITS - 2), j, splits=False)
                square((sq[:, j], resid[:, KT - 2 + j]))

        @block.vector
        def _(dve):
            turn = Turns()
            turn.base[sq_added.name] = 2

            def own(event):
                dve.wait_ge(event, turn.next(event.name))

            BC3 = BC.rearrange("p (a t) -> p a t", a=1)
            CTX_BC3 = CTX_BC.rearrange("p (a t) -> p a t", a=1)

            def seq(ins):
                ins.then_inc(dve_seq, 1)
                dve.wait_ge(dve_seq, turn.next("seq"))

            def tt(dst, a, b, op):
                return dve.tensor_tensor(dst, a, b, op)

            def split(at, j, half=1):
                slot = (2 * j + half) % RING
                dve.wait_ge(hi_done, at.unit(j, 5 + half, 2))
                tt(lo[:, slot], raw[:, slot], hi[:, slot], ALU.subtract).then_inc(lo_done, 1)
                own(lo_done)

            def evac(at, j, dst, splits=True):
                if splits:
                    split(at, j, 0)
                dve.wait_ge(half_copied, at.unit(j, 1))
                tt(dst, G[j % 2][:, 0:T], tmpB[:, j % 2], ALU.add).then_inc(evac_done, 1)
                own(evac_done)

            def mine(at, j):
                dve.wait_ge(evac_done, at.unit(j, 1))

            def low(dst_hi, dst_lo, src, done):
                dve.wait_ge(nt_hi, turn.next("nt"))
                tt(dst_lo, src, dst_hi, ALU.subtract).then_inc(done, 1)
                own(done)

            def diagonal(cols):
                dve.wait_ge(rstd_ready, turn.next("norm"))
                for t in range(2):
                    ins = dve.tensor_scalar(diag[:, t * P:(t + 1) * P], ident[:], rr[:, cols + t:cols + t + 1], None, ALU.mult)
                ins.then_inc(diag_ready, 1)
                own(diag_ready)

            def mean_square(src, n, width=2):
                dve.tensor_scalar(ms[:, 0:width], src, 1.0 / n, EPS, ALU.mult, ALU.add).then_inc(ms_ready, 1)
                own(ms_ready)

            def take_sums(dst, src, add=True):
                dve.wait_ge(sum_ready, turn.next("sum"))
                if add:
                    tt(dst, dst, src, ALU.add).then_inc(sum_taken, 1)
                    own(sum_taken)
                else:
                    dve.tensor_copy(dst, src).then_inc(sum_taken, 1)
                    own(sum_taken)

            def norm_tiles(first, n, gain, shift, src=resid):
                for k in range(first, first + n):
                    ins = dve.scalar_tensor_tensor(t4[:, k % 4], src[:, k], gain(k), BC, ALU.mult, ALU.mult)
                    if shift is None:
                        ins.then_inc(nt_ready, 1)
                        own(nt_ready)
                    else:
                        seq(ins)
                        dve.tensor_scalar(t4[:, k % 4], t4[:, k % 4], shift(k), None, ALU.add).then_inc(nt_ready, 1)
                        own(nt_ready)
                for k in range(first, first + n):
                    low(actA[:, k, 0:T], actA[:, k, T:2 * T], t4[:, k % 4], inA)

            def col(name, k=0, n=1):
                a = VEC[name]
                return vec[:, a + k:a + k + n] if isinstance(k, int) else vec[:, bass.ds(k + a, n)]

            def silu(dst):
                dve.wait_ge(z_exp, turn.next("z"))
                seq(dve.tensor_scalar(ze, ze, 1.0, None, ALU.add))
                seq(dve.reciprocal(ze, ze))
                tt(dst, yz.rearrange("p (a t) -> p a t", a=1), ze.rearrange("p (a t) -> p a t", a=1), ALU.mult)

            def ada_add():
                c = turn.next("chunk", 1)
                dve.wait_ge(ada_summed, turn.value("chunk"))
                both = ADA[:, 0:8].rearrange("p (m r) -> p m r", r=2)
                for r in range(2):
                    four = slice(4 * c, 4 * c + 4) if isinstance(c, int) else bass.ds(c * 4, 4)
                    bias = col("b_ada", c * 4, 4)
                    ins = tt(adav[:, r, four], both[:, :, r], bias, ALU.add)
                ins.then_inc(ada_added, 1)
                own(ada_added)

            def head_max():
                dve.wait_ge(scores_ready, turn.next("head"))
                dve.reduce_max(sm[:, 0:1], S[0][:, 0:P], AX.X)
                seq(dve.reduce_max(sm[:, 1:2], S[0][:, P:3 * P], AX.X))
                dve.scalar_tensor_tensor(sm[:, 2:4], sm[:, 0:2], -1.0, sm[:, 4:6], ALU.mult, ALU.mult).then_inc(negmax_ready, 1)
                own(negmax_ready)

            def head_scale():
                dve.wait_ge(probs_ready, turn.value("head"))
                seq(dve.reciprocal(sm[:, 8:10], sm[:, 6:8]))
                dve.tensor_scalar(P1[:, 0:P], P1[:, 0:P], sm[:, 8:9], None, ALU.mult)
                dve.tensor_scalar(P1[:, P:3 * P], P1[:, P:3 * P], sm[:, 9:10], None, ALU.mult).then_inc(probs_scaled, 1)
                own(probs_scaled)

            def head_body(at, prev, h):
                evac(at, 0, yq)
                if prev:
                    head_max()
                split(at, 0)
                if prev:
                    head_scale()
                evac(at, 1, yk)
                split(at, 1)
                evac(at, 2, yv)
                take_sums(sm[:, 36:40], SUMS, add=False)
                split(at, 2)
                dve.wait_ge(sum_taken, turn.value("sum"))
                mean_square(sm[:, 36:40], HD1, 4)
                diagonal(2)
                dve.tensor_scalar(sm[:, 4:6], rr[:, 0:2], HD1 ** -0.5, None, ALU.mult)
                evac(at, 3, yz)
                ada_add()
                dve.tensor_scalar(qg, yq, col("q_gain"), None, ALU.mult)
                dve.wait_ge(bc_ready, turn.value("norm"))
                dve.scalar_tensor_tensor(kn, yk, col("k_gain"), BC, ALU.mult, ALU.mult).then_inc(qk_ready, 1)
                own(qk_ready)
                split(at, 3)
                silu(z_attn[:, h])
                if prev:
                    take_sums(ss[:, 4:6], SUMS[:, 0:2])

            def attn_tile(i, i_read):
                seq(dve.scalar_tensor_tensor(t4[:, 0:1], y_attn[:, i_read], col("attn_gain", i), BC3, ALU.mult, ALU.mult))
                tt(t4[:, 1:2], t4[:, 0:1], z_attn[:, i_read], ALU.mult).then_inc(nt_ready, 1)
                own(nt_ready)

            def conv_body(at, tail, j, i):
                evac(at, 0, yq)
                if tail:
                    head_max()
                if i is not None:
                    attn_tile(i, bass.ds(i, 1))
                split(at, 0)
                if i is not None:
                    low(actB[:, bass.ds(i, 1), 0:T], actB[:, bass.ds(i, 1), T:2 * T], t4[:, 1:2], inB)
                if tail:
                    head_scale()
                evac(at, 1, yk)
                mine(at, 1)
                tt(upad[:, 2:2 + T], yk, yq, ALU.mult)
                w = VEC["conv_w"]
                seq(dve.tensor_copy(cw, vec[:, w:w + 3] if j is None else vec[:, bass.ds(j * 3 + w, 3)]))
                split(at, 1)
                evac(at, 2, yv)
                seq(dve.tensor_scalar(qg, upad[:, 0:T], cw[:, 0:1], None, ALU.mult))
                seq(dve.scalar_tensor_tensor(qg, upad[:, 1:1 + T], cw[:, 1:2], qg, ALU.mult, ALU.add))
                seq(dve.scalar_tensor_tensor(qg, upad[:, 2:2 + T], cw[:, 2:3], qg, ALU.mult, ALU.add))
                y = y_conv[:, 0:1] if j is None else y_conv[:, bass.ds(j, 1)]
                tt(y, qg.rearrange("p (a t) -> p a t", a=1), yv.rearrange("p (a t) -> p a t", a=1), ALU.mult).then_inc(x_new, 1)
                own(x_new)
                split(at, 2)
                evac(at, 3, yz)
                ada_add()
                split(at, 3)
                silu(z_conv[:, 0:1] if j is None else z_conv[:, bass.ds(j, 1)])
                if tail:
                    take_sums(ss[:, 4:6], SUMS[:, 0:2])
                    dve.wait_ge(sum_taken, turn.value("sum"))
                    mean_square(ss[:, 4:6], HEADS * HD1)
                    diagonal(0)
                take_sums(ss[:, 6:8], SUMS[:, 0:2])
                if tail:
                    dve.wait_ge(bc_ready, turn.value("norm"))

            dve.wait_ge(const_ready, 5)
            dve.wait_ge(small_in, 96)
            dve.wait_ge(act_seq, 2)
            mean_square(ss[:, 0:2], D)
            diagonal(0)
            for n in range(RING):
                dve.wait_ge(hi_done, n + 1)
                tt(lo[:, n], raw[:, n], hi[:, n], ALU.subtract).then_inc(lo_done, 1)
                own(lo_done)
            dve.wait_ge(c_exp, 1)
            seq(dve.tensor_scalar(sm[:, 0:32], sm[:, 0:32], 1.0, None, ALU.add))
            seq(dve.reciprocal(sm[:, 0:32], sm[:, 0:32]))
            for r in range(2):
                tt(cpad[:, :, r], col("c", KT * r, KT), sm[:, KT * r:KT * (r + 1)], ALU.mult).then_inc(c_ready, 1)
                own(c_ready)
            dve.wait_ge(resid_in, 16)
            dve.wait_ge(bc_ready, 1)
            for b in range(4):
                norm_tiles(4 * b, 4, lambda k: col("gain1", k), None)

            head_body(At(0), False, slice(0, 1))
            dve.wait_ge(act_seq, 4)
            mean_square(ss[:, 2:4], D)
            diagonal(0)
            with turn.lap(dve, 7, "dve heads") as i:
                head_body(At(4, 4, i), True, bass.ds(i + 1, 1))
            dve.wait_ge(ada_added, 8)
            for r in range(2):
                dve.scalar_tensor_tensor(scale_a[:, r], adav[:, r, SC_A:SC_A + KT], 1.0, col("norm_attn", 0, KT), ALU.add,
                                         ALU.mult).then_inc(scale_ready, 1)
                own(scale_ready)
            conv_body(At(32), True, None, None)
            with turn.lap(dve, 7, "dve conv") as i:
                conv_body(At(36, 4, i), False, i + 1, i)
            dve.wait_ge(scale_ready, 2)
            attn_tile(7, slice(7, 8))
            low(actB[:, 7:8, 0:T], actB[:, 7:8, T:2 * T], t4[:, 1:2], inB)
            dve.wait_ge(sum_taken, turn.value("sum"))
            mean_square(ss[:, 6:8], CONV_TILES * P)
            diagonal(0)
            dve.wait_ge(bc_ready, turn.value("norm"))
            for b in range(4):
                for k in (2 * b, 2 * b + 1):
                    u, m = k % 2, 1 + k % 2
                    seq(dve.scalar_tensor_tensor(t4[:, 3 * u], y_conv[:, k], col("conv_gain", k), BC, ALU.mult, ALU.mult))
                    tt(t4[:, m], t4[:, 3 * u], z_conv[:, k], ALU.mult).then_inc(nt_ready, 1)
                    own(nt_ready)
                for k in (2 * b, 2 * b + 1):
                    low(actB[:, 8 + k, 0:T], actB[:, 8 + k, T:2 * T], t4[:, 1 + k % 2], inB)

            def add_squares(s):
                dve.wait_ge(sq_ready, turn.next("sqs") + 2 * HEADS + CONV_TILES)
                tt(sqsum[:], sqsum[:], sq[:, s], ALU.add).then_inc(sq_added, 1)
                own(sq_added)

            with turn.lap(dve, 4, "dve w_out") as i:
                at = At(U_OUT1, 4, i)
                for j in range(4):
                    u = bass.ds(i * 4 + j, 1)
                    evac(at, j, t4[:, 0])
                    mine(at, j)
                    if j == 3:
                        ada_add()
                    tt(resid[:, u], resid[:, u], t4[:, 0:1], ALU.add).then_inc(x_new, 1)
                    own(x_new)
                    dve.wait_ge(ctx_full[j], i * 16 + 16)
                    seq(dve.scalar_tensor_tensor(t4[:, 2:3], ctx_raw[:, j:j + 1], scale_a[:, 1, u], CTX_BC3, ALU.mult, ALU.mult))
                    dve.tensor_scalar(t4[:, 3:4], t4[:, 2:3], adav[:, 1, bass.ds(i * 4 + SH_A + j, 1)], None,
                                      ALU.add).then_inc(nt_ready, 1)
                    own(nt_ready)
                    split(at, j)
                    low(actC[:, u, 0:T], actC[:, u, T:2 * T], t4[:, 3:4], inC)
                    add_squares(j % 2)
            take_sums(ss[:, 8:10], SUMS[:, 0:2], add=False)
            dve.wait_ge(sum_taken, turn.value("sum"))
            mean_square(ss[:, 8:10], D)
            seq(dve.memset(sqsum[:], 0.0))
            at = At(U_KV)

            def scaled_rope(y, dst, done=None):
                dve.wait_ge(rot_ready, turn.next("rot"))
                seq(tt(t2b, y, rope[:, 0], ALU.mult))
                tt(t2a, ROT, rope[:, 1], ALU.mult).then_inc(rope_done, 1)
                own(rope_done)
                dve.wait_ge(rope_done, turn.value("rot"))
                ins = tt(dst, t2a, t2b, ALU.add)
                if done is not None:
                    ins.then_inc(done, 1)
                    own(done)

            for n in range(UNITS_KV):
                evac(at, n, kcT[:, n] if n < 2 else y2[:, n % 2])
                split(at, n)
                if n == 0:
                    diagonal(0)
                    dve.wait_ge(bc_ready, turn.value("norm"))
                if n < 4:
                    norm_tiles(4 * n, 4, lambda k: scale_a[:, 0, k:k + 1], lambda k: adav[:, 0, SH_A + k:SH_A + k + 1])
                if n == 5:
                    dve.wait_ge(blk2_in, 48)
                if n in (5, 6):
                    scaled_rope(y2[:, n - 5], kT[:, n - 5])

            def tile_softmax(s):
                for c in ORDER:
                    dve.wait_ge(scores_ready, turn.next("scores") + HEADS)
                    ins = dve.reduce_max(sm[:, c:c + 1], S[c][:], AX.X)
                seq(ins)
                seq(dve.scalar_tensor_tensor(sm[:, 4:8], sm[:, 0:4], HD2 ** -0.5, sm[:, 32:36], ALU.mult, ALU.max))
                seq(tt(sm[:, 12:16], sm[:, 32:36], sm[:, 4:8], ALU.subtract))
                dve.tensor_scalar(sm[:, 8:12], sm[:, 4:8], -1.0, None, ALU.mult).then_inc(negmax_ready, 1)
                own(negmax_ready)

            def tile_scale():
                dve.wait_ge(probs_ready, turn.next("tile") * 4 + HEADS)
                dve.wait_ge(es_ready, turn.value("tile"))
                seq(tt(sm[:, 24:28], sm[:, 20:24], sm[:, 16:20], ALU.add))
                seq(dve.reciprocal(sm[:, 28:32], sm[:, 24:28]))
                for c in ORDER:
                    dve.tensor_scalar(probs[:, c], probs[:, c], sm[:, 28 + c:29 + c], None, ALU.mult).then_inc(probs_scaled, 1)
                    own(probs_scaled)

            def slot(at, s, dst, before, last, sink=None, out_tile=None, ada=False):
                evac(at, s, dst)
                if before:
                    for t in range(2):
                        dve.wait_ge(p_turned, turn.next("p_turned") * 2 + HEADS)
                        dve.tensor_copy(turned[:, 1, :, t * P:(t + 1) * P],
                                        S[2 + t][:].rearrange("p (k t) -> p k t", k=4)).then_inc(p_copied2, 1)
                        own(p_copied2)
                if last:
                    scaled_rope(y2[:, 1 - s], qr, qr_ready)
                    seq(dve.tensor_copy(sm[:, 32:36], sinks[:, sink]))
                if before:
                    low(actB[:, out_tile, 0:T], actB[:, out_tile, T:2 * T], M[:, 0:T].rearrange("p (a t) -> p a t", a=1), inB)
                if last:
                    tile_softmax(1 - s)
                split(at, s)
                if last:
                    tile_scale()
                if ada and s == 1:
                    ada_add()

            at = At(U_Q)
            evac(at, 0, y2[:, 0])
            split(at, 0)
            slot(at, 1, y2[:, 1], False, True, slice(0, 4), ada=True)
            with turn.lap(dve, 3, "dve q") as i:
                at = At(U_Q + 2, 2, i)
                slot(at, 0, y2[:, 0], True, True, bass.ds(i * 8 + 4, 4), bass.ds(i, 1), ada=True)
                slot(at, 1, y2[:, 1], True, True, bass.ds(i * 8 + 8, 4), bass.ds(i + 4, 1), ada=True)
            at = At(U_POOL)
            inner = slice(PAD, PAD + T)
            dve.wait_ge(sink_ready, 1)
            slot(at, 0, upad2[:, 0, inner], True, True, slice(28, 32), slice(3, 4))
            slot(at, 1, upad2[:, 1, inner], True, False, None, slice(7, 8))

            def window(g):
                w = WINDOWS[g]
                if g:
                    dve.wait_ge(pool_ready, g)
                for m in range(2):
                    src, bufs, width, length = upad2[:, m], (wsA, wsB), 1, T + 2 * PAD
                    while width < w:
                        length -= width
                        dst = bufs[0]
                        seq(tt(dst[:, 0:length], src[:, 0:length], src[:, width:width + length], ALU.add))
                        src, bufs, width = dst, bufs[::-1], 2 * width
                    at0 = PAD - w // 2
                    other = bufs[0]
                    seq(tt(other[:, 0:T], src[:, at0:at0 + T], inv_count[:, g], ALU.mult))
                    ins = tt(pooled[:, m], other[:, 0:T], upad2[:, m, inner], ALU.subtract)
                    if m == 0:
                        seq(ins)
                ins.then_inc(pooled_ready, 1)
                own(pooled_ready)

            def pool_out(g):
                dve.wait_ge(pool_ready, g + 1)
                for m in range(2):
                    dve.tensor_scalar(t4[:, m], S[m][:, 0:T], col("pool_scale", 2 * g + m), None, ALU.mult).then_inc(nt_ready, 1)
                    own(nt_ready)
                for m in range(2):
                    k = 8 + 2 * g + m
                    low(actB[:, k, 0:T], actB[:, k, T:2 * T], t4[:, m], inB)

            mine(at, 1)
            window(0)
            for n in range(2, UNITS_U):
                evac(at, n, upad2[:, n % 2, inner])
                split(at, n)
                if n % 2 == 0:
                    pool_out(n // 2 - 1)
                else:
                    mine(at, n)
                    window(n // 2)
            pool_out(3)
            dve.scalar_tensor_tensor(scale_m[:], adav[:, 0, SC_M:SC_M + KT], 1.0, col("norm_mlp", 0, KT), ALU.add,
                                     ALU.mult).then_inc(scale_ready, 1)
            own(scale_ready)

            with turn.lap(dve, 4, "dve w_out_2") as i:
                at = At(U_OUT2, 4, i)
                for j in range(4):
                    u = bass.ds(i * 4 + j, 1)
                    evac(at, j, t4[:, 2 + j % 2])
                    mine(at, j)
                    dve.scalar_tensor_tensor(resid[:, u], t4[:, 2 + j % 2:3 + j % 2], adav[:, 0, bass.ds(i * 4 + G_A + j, 1)],
                                             resid[:, u], ALU.mult, ALU.add).then_inc(x_new, 1)
                    own(x_new)
                    split(at, j)
                    add_squares(j % 2)
            take_sums(ss[:, 8:10], SUMS[:, 0:2], add=False)
            dve.wait_ge(sum_taken, turn.value("sum"))
            mean_square(ss[:, 8:10], D)
            seq(dve.memset(sqsum[:], 0.0))
            diagonal(0)
            dve.wait_ge(scale_ready, 3)
            dve.wait_ge(bc_ready, turn.value("norm"))
            for b in range(4):
                norm_tiles(4 * b, 4, lambda k: scale_m[:, k:k + 1], lambda k: adav[:, 0, SH_M + k:SH_M + k + 1])

            for g in range(MLP_GROUPS):
                base = U_MLP + 2 * KT * g
                with turn.lap(dve, 8, "dve up") as i:
                    for j in range(2):
                        at, u = At(base, 2, i), bass.ds(i * 2 + j, 1)
                        evac(at, j, t4[:, j])
                        mine(at, j)
                        dve.scalar_tensor_tensor(t4[:, 2 + j], t4[:, j], 0.0, t4[:, j], ALU.max, ALU.mult).then_inc(nt_ready, 1)
                        own(nt_ready)
                        split(at, j)
                        low(actB[:, u, 0:T], actB[:, u, T:2 * T], t4[:, 2 + j:3 + j], inB)

                def down(at, j, u, splits, gate):
                    evac(at, j, t4[:, j], splits)
                    mine(at, j)
                    if gate is None:
                        tt(acc[:, u], acc[:, u], t4[:, j:j + 1], ALU.add)
                    else:
                        seq(tt(t4[:, 2 + j:3 + j], acc[:, u], t4[:, j:j + 1], ALU.add))
                        dve.scalar_tensor_tensor(resid[:, u], t4[:, 2 + j:3 + j], gate, resid[:, u], ALU.mult,
                                                 ALU.add).then_inc(x_new, 1)
                        own(x_new)
                    if splits:
                        split(at, j)
                    if gate is not None:
                        add_squares(j)

                if g == 0:
                    dve.wait_ge(acc_zero, 1)
                if g < MLP_GROUPS - 1:
                    with turn.lap(dve, 8, "dve down") as i:
                        for j in range(2):
                            down(At(base + KT, 2, i), j, bass.ds(i * 2 + j, 1), True, None)
                else:
                    with turn.lap(dve, 7, "dve last down") as i:
                        for j in range(2):
                            down(At(base + KT, 2, i), j, bass.ds(i * 2 + j, 1), True,
                                 adav[:, 0, bass.ds(i * 2 + G_M + j, 1)])
                    for j in range(2):
                        k = KT - 2 + j
                        down(At(UNITS - 2), j, slice(k, k + 1), False, adav[:, 0, G_M + k:G_M + k + 1])

            take_sums(ss[:, 8:10], SUMS[:, 0:2], add=False)
            dve.wait_ge(sum_taken, turn.value("sum"))
            mean_square(ss[:, 8:10], D)
            diagonal(0)
            dve.wait_ge(bc_ready, turn.value("norm"))
            for k in range(KT):
                dve.scalar_tensor_tensor(resid[:, k], resid[:, k], col("final", k), BC, ALU.mult, ALU.mult).then_inc(out_ready, 1)
                own(out_ready)


def _units(w):
    n = w.shape[1] // P
    w = w.reshape(2, KT // 2, P, n, P).transpose(3, 0, 2, 1, 4)
    return w.reshape(2 * n, P, HALF)


def _interleave(*parts):
    n = parts[0].shape[0] // 2
    return np.stack([p.reshape(n, 2, P, HALF) for p in parts], axis=1).reshape(-1, P, HALF)


def _tiles(v):
    return v.reshape(-1, P).T


def constants():
    ident = np.eye(P, dtype=np.float32)
    sel = (np.arange(P)[:, None] % 32 == np.arange(2)).astype(np.float32)
    q, k = np.arange(P)[:, None], np.arange(P)[None, :]
    far = np.float32(-1e30)
    masks = np.stack([ident, np.where(k <= q, 0, far), np.where(k + P - q <= 128, 0, far), np.where(q + P - k <= 128, 0, far)], 1)
    half = HD2 // 2
    inv_freq = (np.float32(10000.0) ** (-np.arange(0, half, 2, dtype=np.float32) / np.float32(half))).astype(np.float32)
    pos = np.stack([np.arange(T) // 64, np.arange(T) % 64]).astype(np.float32)
    ang = pos[:, None, :] * inv_freq[None, :, None]
    ang = np.stack([ang, ang], 1).reshape(HD2, T)
    ang = np.concatenate([ang, ang])
    rope = np.stack([np.cos(ang), np.sin(ang)], 1).astype(np.float32)
    rot = np.zeros((P, P), np.float32)
    for f in range(P):
        if f % 32 < 16:
            rot[f + 16, f] = -1.0
        else:
            rot[f - 16, f] = 1.0
    t = np.arange(T)
    inv = [1.0 / (np.clip(t - w // 2 + w, 0, T) - np.clip(t - w // 2, 0, T)) for w in WINDOWS]
    inv = np.broadcast_to(np.stack(inv).astype(np.float32), (P, 4, T))
    return ident, sel, masks, rope, rot, np.ascontiguousarray(inv)


def kernel(**inputs):
    import ml_dtypes
    import concourse.bacc as _bacc
    from concourse.bass_utils import run_bass_kernel_spmd as _run

    a = {k: np.asarray(v) for k, v in inputs.items()}
    ident, sel, masks, rope, rot, inv_count = constants()

    w_in = _units(a["w_in"][0]).reshape(8, 8, 2, P, HALF)
    h, b, c, z, q, k, v, za = (w_in[i].reshape(16, P, HALF) for i in range(8))
    w_out = a["w_out"][0]
    w_out = np.concatenate([w_out[1024:], w_out[:1024]])
    w2 = a["w_in_2"][0]
    wq = w2[:, :1024].reshape(D, 2, 2, 4, HD2).transpose(0, 3, 1, 2, 4)
    wq = _units(wq.reshape(D, 1024))
    kv = _units(w2[:, 1024:1536])
    w_out2 = a["w_out_2"][0]
    mixed = w_out2[:1024].reshape(2, 2, 4, HD2, D).transpose(0, 2, 1, 3, 4).reshape(1024, D)
    w_out2 = np.concatenate([mixed, w_out2[1024:]])
    up, down = a["w_mlp_up_2"][0], a["w_mlp_down_2"][0]
    mlp = []
    for g in range(MLP_GROUPS):
        mlp += [_units(up[:, g * D:(g + 1) * D]), _units(down[g * D:(g + 1) * D])]
    stream = np.concatenate([_interleave(q, k, v, za), _interleave(h, c, b, z), _units(w_out), kv, kv, wq,
                             _units(w2[:, 1536:]), _units(w_out2)] + mlp)
    w_ada = a["w_ada_2"][0].reshape(4, 4, P, 24, 512).transpose(3, 0, 2, 1, 4).reshape(96, P, D)
    conv_w = a["conv_w"][0].reshape(3, 8, P).transpose(2, 1, 0).reshape(P, 24)
    vec = np.concatenate([_tiles(a["norm_gain"][0]), conv_w, _tiles(a["conv_out_gain"][0]), _tiles(a["attn_out_gain"][0]),
                          _tiles(a["q_norm_gain"][0]), _tiles(a["k_norm_gain"][0]), _tiles(a["norm_attn_w_2"][0]),
                          _tiles(a["norm_mlp_w_2"][0]), _tiles(a["b_ada_2"][0]), _tiles(a["pool_scale_2"][0]),
                          _tiles(a["final_norm_w_2"]), _tiles(a["c_2"][0]), _tiles(a["c_ctx_2"])], axis=1)
    sinks = a["attn_sink_2"][0].reshape(2, 2, 4).transpose(2, 0, 1).reshape(4, 2, 2, 1)
    sinks = np.broadcast_to(np.broadcast_to(sinks, (4, 2, 2, 2)).reshape(32), (P, 32))
    x, cx = a["x"][0], a["ctx_2"][0]
    feed = {
        "stream": stream, "w_ada": w_ada, "vec": vec, "ident": ident, "ones": np.ones((P, P), np.float32), "sel": sel,
        "sinks": sinks, "masks": masks.astype(ml_dtypes.bfloat16), "rope": rope, "rot": rot, "inv_count": inv_count,
        "x_tok": x.reshape(2, P, D).transpose(1, 0, 2), "ctx_tok": cx.reshape(2, P, D).transpose(1, 0, 2),
        "xT": x.reshape(T, KT, P).transpose(2, 1, 0), "ctxT": cx.reshape(T, KT, P).transpose(2, 1, 0),
        "pool_w": a["pool_w_2"][0].reshape(4, 2, P, 256).transpose(2, 0, 1, 3),
    }
    nc = _bacc.Bacc("TRN2", target_bir_lowering=False, num_devices=1)
    arrays, aps = {}, {}
    for name, array in feed.items():
        arrays[name + "_dram"] = np.ascontiguousarray(array)
        aps[name] = nc.dram_tensor(name + "_dram", array.shape, mybir.dt.from_np(array.dtype), kind="ExternalInput").ap()
    out = nc.dram_tensor("out_dram", (P, KT, T), F32, kind="ExternalOutput").ap()
    program(nc, aps, out)
    r = _run(nc, [arrays], core_ids=[0])
    got = r.results[0]["out_dram"]
    return np.ascontiguousarray(got.transpose(2, 1, 0)).reshape(1, T, D)
```
